# Optimizing a Trainium2 kernel written in Bass

```python
import math
import jax, jax.numpy as jnp
from jax import lax
import numpy as np

D_MODEL = 1024
BATCH = 1
SEQ = 256
DEPTH = 2

CHUNK = 64
HEAD_DIM = 64
RWKV_HEADS = 8
SB_HEADS = 8
RWKV_W = RWKV_HEADS * HEAD_DIM
SB_W = SB_HEADS * HEAD_DIM
D_MIX = RWKV_W + SB_W
DECAY_RANK = 32
ICLR_RANK = 32
VRES_RANK = 32
GATE_RANK = 96
D_FF = 3584
N_EXPERTS = 8
TOP_K = 2
SB_BLOCK = 128
NORM_EPS = 1e-6
LNX_EPS = 64e-5
DECAY_SCALE = math.exp(-0.5)

kernel_name = 'hybrid_rwkv7_stickbreaking_moe_block'

def _rwkv_cols(has_vres):
    return 3 * RWKV_W + DECAY_RANK + ICLR_RANK + GATE_RANK + (VRES_RANK if has_vres else 0)

def _rmsnorm(x, g):
    xf = x.astype(jnp.float32)
    y = xf * lax.rsqrt(jnp.mean(xf * xf, axis=-1, keepdims=True) + NORM_EPS)
    return (y * g.astype(jnp.float32)).astype(x.dtype)

def _heads(t, n_heads):
    return t.reshape(t.shape[:-1] + (n_heads, t.shape[-1] // n_heads))

def _token_shift(p, mu):
    prev = jnp.pad(p, ((0, 0), (1, 0), (0, 0)))[:, :-1]
    return p + mu * (prev - p)

def _rwkv7_scan(r, w, k, v, z, b):
    def step(S, inp):
        r_t, w_t, k_t, v_t, z_t, b_t = inp
        Sz = jnp.einsum('bhvk,bhk->bhv', S, z_t)
        S = S * w_t[:, :, None, :] + Sz[..., None] * b_t[:, :, None, :] + v_t[..., None] * k_t[:, :, None, :]
        return S, jnp.einsum('bhvk,bhk->bhv', S, r_t)
    B, T, H, N = r.shape
    xs = (jnp.moveaxis(r, 1, 0), jnp.moveaxis(w, 1, 0), jnp.moveaxis(k, 1, 0),
          jnp.moveaxis(v, 1, 0), jnp.moveaxis(z, 1, 0), jnp.moveaxis(b, 1, 0))
    _, ys = lax.scan(step, jnp.zeros((B, H, N, N), jnp.float32), xs)
    return jnp.moveaxis(ys, 0, 1)

def _rwkv7_group(proj, p, v_first):
    f32 = jnp.float32
    has_vres = v_first is not None
    sizes = [RWKV_W] * 3 + [DECAY_RANK, ICLR_RANK, GATE_RANK] + ([VRES_RANK] if has_vres else [])
    parts = jnp.split(_token_shift(proj, p['mu']), [int(o) for o in np.cumsum(sizes)[:-1]], axis=-1)
    r, k, v, w_dn, a_dn, g_dn = parts[:6]
    decay = jnp.exp(-DECAY_SCALE * jax.nn.sigmoid((p['decay0'] + jnp.tanh(w_dn) @ p['decay_up']).astype(f32)))
    iclr = jax.nn.sigmoid((p['iclr0'] + a_dn @ p['iclr_up']).astype(f32))
    gate = (jax.nn.sigmoid(g_dn) @ p['gate_up']).astype(f32)
    if has_vres:
        v = v + (v_first - v) * jax.nn.sigmoid(p['vres0'] + parts[6] @ p['vres_up'])
    else:
        v_first = v
    r, k, v = r.astype(f32), k.astype(f32), v.astype(f32)
    kk = _heads(k * p['k_k'], RWKV_HEADS)
    kk = kk * lax.rsqrt(jnp.maximum(jnp.sum(kk * kk, axis=-1, keepdims=True), 1e-12))
    k = k * (1.0 + (iclr - 1.0) * p['k_a'])
    rh, kh, vh = _heads(r, RWKV_HEADS), _heads(k, RWKV_HEADS), _heads(v, RWKV_HEADS)
    wh, ah = _heads(decay, RWKV_HEADS), _heads(iclr, RWKV_HEADS)
    y = _rwkv7_scan(rh, wh, kh, vh, -kk, kk * ah)
    mean = jnp.mean(y, axis=-1, keepdims=True)
    var = jnp.mean(jnp.square(y - mean), axis=-1, keepdims=True)
    y = ((y - mean) * lax.rsqrt(var + LNX_EPS)).reshape(r.shape) * p['lnx_g'] + p['lnx_b']
    bonus = (jnp.sum(rh * kh * p['r_k'], axis=-1, keepdims=True) * vh).reshape(r.shape)
    return (y + bonus) * gate, v_first

def _stick_breaking(q, k, v):
    B, T, H, N = q.shape
    f32 = jnp.float32
    qh = jnp.transpose(q, (0, 2, 1, 3)).astype(f32) * (N ** -0.5)
    kh = jnp.transpose(k, (0, 2, 1, 3)).astype(f32)
    vh = jnp.transpose(v, (0, 2, 1, 3)).astype(f32)
    nb = T // SB_BLOCK
    q_blocks = jnp.transpose(qh.reshape(B, H, nb, SB_BLOCK, N), (2, 0, 1, 3, 4))
    kpos = jnp.arange(T)

    def block(args):
        qb, i = args
        qpos = i * SB_BLOCK + jnp.arange(SB_BLOCK)
        z = jnp.einsum('bhqd,bhkd->bhqk', qb, kh)
        mask = kpos[None, :] < qpos[:, None]
        log_keep = jnp.where(mask, jax.nn.log_sigmoid(-z), 0.0)
        between = lax.cumsum(log_keep, axis=3, reverse=True) - log_keep
        att = jnp.where(mask, jnp.exp(jax.nn.log_sigmoid(z) + between), 0.0)
        return jnp.einsum('bhqk,bhkd->bhqd', att, vh)

    o = lax.map(block, (q_blocks, jnp.arange(nb)))
    return jnp.transpose(o, (1, 0, 3, 2, 4)).reshape(B, T, H, N)

def _mixer(h, p, v_first):
    proj = h @ p['w_in']
    n_rwkv = p['mu'].shape[0]
    y_a, v_first = _rwkv7_group(proj[..., :n_rwkv], p, v_first)
    q, k, v = jnp.split(proj[..., n_rwkv:], 3, axis=-1)
    o = _stick_breaking(_heads(q, SB_HEADS), _heads(k, SB_HEADS), _heads(v, SB_HEADS))
    o = o * lax.rsqrt(jnp.mean(o * o, axis=-1, keepdims=True) + NORM_EPS)
    y_b = o.reshape(h.shape[:-1] + (SB_W,)) * p['sb_g']
    y = jnp.concatenate([y_a, y_b], axis=-1).astype(h.dtype) @ p['w_out']
    return y, v_first

def _swiglu(h, w_gate, w_up, w_down):
    return (jax.nn.silu(h @ w_gate) * (h @ w_up)) @ w_down

def _moe(h, router, w_gate, w_up, w_down):
    B, T, D = h.shape
    hf = h.reshape(B * T, D)
    logits = (hf @ router).astype(jnp.float32)
    top_v, top_i = lax.top_k(logits, TOP_K)
    gates = jax.nn.softmax(top_v, axis=-1)
    dense_gate = jnp.sum(jax.nn.one_hot(top_i, N_EXPERTS, dtype=jnp.float32) * gates[..., None], axis=1)
    dense_gate = dense_gate.astype(h.dtype)
    out = jnp.zeros_like(hf)
    for e in range(N_EXPERTS):
        out = out + dense_gate[:, e:e + 1] * _swiglu(hf, w_gate[e], w_up[e], w_down[e])
    return out.reshape(B, T, D)

def _gain(key, n):
    return 1.0 + 0.05 * jax.random.normal(key, (n,), jnp.float32)

def _normal(key, shape, scale):
    return scale * jax.random.normal(key, shape, jnp.float32)

def _init_layer(key, l):
    ks = jax.random.split(key, 24)
    has_vres = l > 0
    n_rwkv = _rwkv_cols(has_vres)
    s = '_' + str(l)
    p = {}
    p['mix_pre' + s] = _gain(ks[0], D_MODEL)
    p['w_in' + s] = _normal(ks[1], (D_MODEL, n_rwkv + 3 * SB_W), D_MODEL ** -0.5)
    p['mu' + s] = jax.random.uniform(ks[2], (n_rwkv,), jnp.float32)
    p['decay0' + s] = _normal(ks[3], (RWKV_W,), 1.0)
    p['decay_up' + s] = _normal(ks[4], (DECAY_RANK, RWKV_W), DECAY_RANK ** -0.5)
    p['iclr0' + s] = _normal(ks[5], (RWKV_W,), 0.5)
    p['iclr_up' + s] = _normal(ks[6], (ICLR_RANK, RWKV_W), ICLR_RANK ** -0.5)
    p['gate_up' + s] = _normal(ks[7], (GATE_RANK, RWKV_W), GATE_RANK ** -0.5)
    if has_vres:
        p['vres0' + s] = _normal(ks[8], (RWKV_W,), 0.5)
        p['vres_up' + s] = _normal(ks[9], (VRES_RANK, RWKV_W), VRES_RANK ** -0.5)
    p['k_k' + s] = 0.85 + _normal(ks[10], (RWKV_W,), 0.05)
    p['k_a' + s] = 1.0 + _normal(ks[11], (RWKV_W,), 0.05)
    p['r_k' + s] = _normal(ks[12], (RWKV_HEADS, HEAD_DIM), 0.1)
    p['lnx_g' + s] = _gain(ks[13], RWKV_W)
    p['lnx_b' + s] = _normal(ks[14], (RWKV_W,), 0.02)
    p['sb_g' + s] = _gain(ks[15], SB_W)
    p['w_out' + s] = _normal(ks[16], (D_MIX, D_MODEL), D_MIX ** -0.5)
    p['mix_post' + s] = _gain(ks[17], D_MODEL)
    p['ffn_pre' + s] = _gain(ks[18], D_MODEL)
    if l % 2 == 0:
        p['ff_gate' + s] = _normal(ks[19], (D_MODEL, D_FF), D_MODEL ** -0.5)
        p['ff_up' + s] = _normal(ks[20], (D_MODEL, D_FF), D_MODEL ** -0.5)
        p['ff_down' + s] = _normal(ks[21], (D_FF, D_MODEL), D_FF ** -0.5)
    else:
        p['router' + s] = _normal(ks[19], (D_MODEL, N_EXPERTS), D_MODEL ** -0.5)
        p['moe_gate' + s] = _normal(ks[20], (N_EXPERTS, D_MODEL, D_FF), D_MODEL ** -0.5)
        p['moe_up' + s] = _normal(ks[21], (N_EXPERTS, D_MODEL, D_FF), D_MODEL ** -0.5)
        p['moe_down' + s] = _normal(ks[22], (N_EXPERTS, D_FF, D_MODEL), D_FF ** -0.5)
    p['ffn_post' + s] = _gain(ks[23], D_MODEL)
    return p

def setup_inputs(seed: int = 0) -> dict:
    key = jax.random.key(seed)
    ks = jax.random.split(key, DEPTH + 1)
    params = {'x': jax.random.normal(ks[0], (BATCH, SEQ, D_MODEL), jnp.float32)}
    for l in range(DEPTH):
        params.update(_init_layer(ks[l + 1], l))
    return params

def reference(x,
              mix_pre_0, w_in_0, mu_0, decay0_0, decay_up_0, iclr0_0, iclr_up_0, gate_up_0,
              k_k_0, k_a_0, r_k_0, lnx_g_0, lnx_b_0, sb_g_0, w_out_0, mix_post_0,
              ffn_pre_0, ff_gate_0, ff_up_0, ff_down_0, ffn_post_0,
              mix_pre_1, w_in_1, mu_1, decay0_1, decay_up_1, iclr0_1, iclr_up_1, gate_up_1,
              vres0_1, vres_up_1,
              k_k_1, k_a_1, r_k_1, lnx_g_1, lnx_b_1, sb_g_1, w_out_1, mix_post_1,
              ffn_pre_1, router_1, moe_gate_1, moe_up_1, moe_down_1, ffn_post_1):
    layers = [
        dict(mix_pre=mix_pre_0, w_in=w_in_0, mu=mu_0, decay0=decay0_0, decay_up=decay_up_0,
             iclr0=iclr0_0, iclr_up=iclr_up_0, gate_up=gate_up_0, k_k=k_k_0, k_a=k_a_0,
             r_k=r_k_0, lnx_g=lnx_g_0, lnx_b=lnx_b_0, sb_g=sb_g_0, w_out=w_out_0,
             mix_post=mix_post_0, ffn_pre=ffn_pre_0, ffn=(ff_gate_0, ff_up_0, ff_down_0),
             ffn_post=ffn_post_0),
        dict(mix_pre=mix_pre_1, w_in=w_in_1, mu=mu_1, decay0=decay0_1, decay_up=decay_up_1,
             iclr0=iclr0_1, iclr_up=iclr_up_1, gate_up=gate_up_1, vres0=vres0_1, vres_up=vres_up_1,
             k_k=k_k_1, k_a=k_a_1, r_k=r_k_1, lnx_g=lnx_g_1, lnx_b=lnx_b_1, sb_g=sb_g_1,
             w_out=w_out_1, mix_post=mix_post_1, ffn_pre=ffn_pre_1,
             ffn=(router_1, moe_gate_1, moe_up_1, moe_down_1), ffn_post=ffn_post_1),
    ]
    v_first = None
    for l in range(DEPTH):
        p = layers[l]
        y, v_first = _mixer(_rmsnorm(x, p['mix_pre']), p, v_first)
        x = x + _rmsnorm(y, p['mix_post'])
        hn = _rmsnorm(x, p['ffn_pre'])
        f = _swiglu(hn, *p['ffn']) if l % 2 == 0 else _moe(hn, *p['ffn'])
        x = x + _rmsnorm(f, p['ffn_post'])
    return x


_drawn_inputs = setup_inputs


def setup_inputs(seed=0):
    import zlib

    import numpy as np

    out = dict(_drawn_inputs(seed))
    spreads = {}
    factors = {}
    for name, (base, spread) in spreads.items():
        noise = np.random.default_rng([zlib.crc32(name.encode()), seed]).standard_normal(out[name].shape)
        drawn = base * np.exp(spread * noise) if base else spread * noise
        out[name] = __import__('jax').numpy.asarray(drawn.astype(out[name].dtype))
    for name, factor in factors.items():
        out[name] = (out[name] * factor).astype(out[name].dtype)
    return out
```

```python
import math
from contextlib import ExitStack

import numpy as np
import concourse.bass as bass
import concourse.mybir as mybir

F32, F32R, I32 = mybir.dt.float32, mybir.dt.float32r, mybir.dt.int32
ALU, ACT, AX = mybir.AluOpType, mybir.ActivationFunctionType, mybir.AxisListType

P = 128
TOK, D, F = 256, 1024, 3584
TT = TOK // P
KD = D // P
HD = 64
RW = 512
G = RW // P
NSB = 8
LO_WA, LO_G = 64, 96
RANK = 32
NE, MAX_ITEMS = 8, 11
FT = 256
NF = F // FT
MID = 63
LEVELS = 7
DECAY_SCALE = math.exp(-0.5)
NORM_EPS, LNX_EPS = 1e-6, 64e-5
MASKED = -1e30

ROW = dict(mu=0, decay0=14, iclr0=18, vres0=22, k_k=26, k_a=30, r_k=34, lnx_g=38, lnx_b=42, sb_g=46,
           mix_pre=50, ffn_pre=58)
NROWS = 66

LAYER_INPUTS = ["mix_pre", "w_in", "mu", "decay0", "decay_up", "iclr0", "iclr_up", "gate_up", "k_k",
                "k_a", "r_k", "lnx_g", "lnx_b", "sb_g", "w_out", "mix_post", "ffn_pre"]
INPUTS = (["x"] + [n + "_0" for n in LAYER_INPUTS + ["ff_gate", "ff_up", "ff_down", "ffn_post"]]
          + [n + "_1" for n in LAYER_INPUTS + ["vres0", "vres_up", "router", "moe_gate", "moe_up",
                                               "moe_down", "ffn_post"]])

SIGNALS = """x_loaded params_loaded zeroed consts cols_mm cols_ready coef_ready ups_zero ups_loaded
post_loaded gpre_loaded router_loaded
sq_done ms_done rstd_done xn_ready xT_mm xT_act xT_dve
mw_loaded0 mw_loaded1 proj_mm shift_act shifted sb_copied lw_ready
upA_mm dec_done upB_mm gate_done v_ready
kkr_done kksq_done kkn_mm nn_done rn_done cd_done decays_done bkzr_done rr_done bonus_mm bonus_done
tok_mm tok_ready score_mm score_ready asT_done y_mm y_copied g_mm d_ready
solve_mm solve_act solve_dve yT_act yT_dve
z_mm softplus_ln spm_done arg_mm arg_done att_exp att_done o_mm o_copied
mean_mm centred sq2_done var_mm rs_done mixed wo_mm post_sq post_ms post_rstd x_ready
ff_gu_loaded0 ff_gu_loaded1 ff_d_loaded0 ff_d_loaded1 ff_gu_hi ff_gu_lo ff_d_hi ff_d_lo
ff_gu_mm ff_silu ff_h_done ff_tr_mm ff_hT_hi ff_hT_lo ff_dn_mm
moe_gu_loaded0 moe_gu_loaded1 moe_d_loaded0 moe_d_loaded1 moe_gu_hi moe_gu_lo moe_d_hi moe_d_lo
moe_gu_mm moe_silu moe_h_done moe_tr_mm moe_hT_hi moe_hT_lo moe_dn_mm
router_mm logits_done picks_done gates_exp counts_mm table_ready hn_ready
sel_done gather_mm xg_hi xg_lo sel_t_mm sel_t_done y_evicted scatter_mm acc_added out_done
dve_step act_step pool_step""".split()


class Stream:

    def __init__(self, s, part, token_tiles, slot0, credit):
        self.T, self.slot0, self.credit = token_tiles, slot0, credit
        self.gu_loaded = [s[part + "gu_loaded0"], s[part + "gu_loaded1"]]
        self.d_loaded = [s[part + "d_loaded0"], s[part + "d_loaded1"]]
        self.gu_hi = s[part + "gu_hi"]
        self.gu_lo = s[part + "gu_lo"]
        self.d_hi = s[part + "d_hi"]
        self.d_lo = s[part + "d_lo"]
        self.gu_mm = s[part + "gu_mm"]
        self.silu = s[part + "silu"]
        self.h_done = s[part + "h_done"]
        self.tr_mm = s[part + "tr_mm"]
        self.hT_hi = s[part + "hT_hi"]
        self.hT_lo = s[part + "hT_lo"]
        self.dn_mm = s[part + "dn_mm"]


def build(nc, a, out):
    with ExitStack() as ctx:
        s = {n: ctx.enter_context(nc.semaphore(n)) for n in SIGNALS}
        mw_loaded = [s["mw_loaded0"], s["mw_loaded1"]]
        bank = [ctx.enter_context(nc.psum_tensor(f"bank{i}", [P, 512], F32)) for i in range(8)]

        top = [-(-nc.sbuf_base // 32) * 32]

        starts = {}

        def place(at, *tensors):
            made = []
            for name, shape, dt in tensors:
                at = -(-at // 32) * 32
                starts[name] = at
                made.append(nc.alloc_sbuf_tensor_at(name, [P, *shape], dt, offset=at))
                at += 4 * int(np.prod(shape))
            top[0] = max(top[0], -(-at // 32) * 32)
            return made

        def after(*tensors):
            return place(top[0], *tensors)

        x, = after(("x", [TT, D], F32))
        at = top[0]
        xn, = place(at, ("xn", [TT, D], F32))
        yo, = place(at, ("yo", [KD, TOK], F32))
        at = top[0]
        xnT, = place(at, ("xnT", [KD, TOK], F32))
        xT_hi, = place(at, ("xT_hi", [KD, TOK], F32R))
        rows0, rows1 = place(at, ("rows0", [P], F32), ("rows1", [P], F32))
        at = top[0]
        xT_lo, = place(at, ("xT_lo", [KD, TOK], F32R))
        acc, = place(at, ("acc", [TT, D], F32))
        vr, vdiff = place(at, ("vr", [G, TOK], F32), ("vdiff", [G, TOK], F32))
        xg_lo, = after(("xg_lo", [KD, P], F32R))
        at = top[0]
        vf, = place(at, ("vf", [G, TOK], F32))
        gpre, = place(at, ("gpre", [D], F32))
        gpost, = after(("gpost", [D], F32))
        ident, ones, neg_ones, heads1, heads64, iota1, eps = after(
            ("ident", [P], F32), ("ones", [P], F32), ("neg_ones", [P], F32), ("heads1", [P], F32),
            ("heads64", [P], F32), ("iota1", [P], F32), ("eps", [2], F32))
        cols0, cols1, coef0, coef1 = after(("cols0", [NROWS], F32), ("cols1", [NROWS], F32),
                                           ("coef0", [18], F32), ("coef1", [18], F32))
        ss, ms, rstd, pss, router = after(("ss", [TT], F32), ("ms", [TT], F32), ("rstd", [TT], F32),
                                          ("pss", [TT, 2], F32), ("router", [KD, NE], F32))
        up_mask, = after(("up_mask", [2, P], F32))
        at = top[0]
        level1, levelT, neg_low, neg_mask = place(
            at, ("level1", [P], F32), ("levelT", [LEVELS, P], F32), ("neg_low", [P], F32),
            ("neg_mask", [P], F32))
        sel, selg, selT = place(at, ("sel", [TT, P], F32), ("selg", [TT, P], F32),
                                ("selT", [TT, P], F32))
        at = top[0]
        up_dec, up_icl, up_gate, up_vres = place(at, ("up_dec", [RW], F32), ("up_icl", [RW], F32),
                                                 ("up_gate", [RW], F32), ("up_vres", [RW], F32))
        silu, h, hT_hi, hT_lo = place(at, ("silu", [2, FT], F32), ("h", [2, FT], F32),
                                      ("hT_hi", [2, 2, P], F32R), ("hT_lo", [2, 2, P], F32R))
        y_sb, = place(at, ("y_sb", [D], F32))
        route, counts, item_pos, item_sel, item_gate, table = after(
            ("route", [10, 2 * NE], F32), ("counts", [4, NE], F32), ("item_pos", [TT, 12], F32),
            ("item_sel", [TT, 12], F32), ("item_gate", [TT, 12], F32), ("table", [16], I32))
        raw_gu, = after(("raw_gu", [2, KD, 2 * FT], F32))
        at = top[0]
        raw_d, = place(at, ("raw_d", [2, 2, D], F32))
        sig, cum, pdec, rn = place(at, ("sig", [G, TOK], F32), ("cum", [G, TOK], F32),
                                   ("pdec", [G, TOK], F32), ("rn", [G, TOK], F32))
        at = top[0]
        gu_hi, gu_lo, d_hi, d_lo = place(
            at, ("gu_hi", [2, KD, 2 * FT], F32R), ("gu_lo", [2, KD, 2 * FT], F32R),
            ("d_hi", [2, 2, D], F32R), ("d_lo", [2, 2, D], F32R))
        (rkv, lw, sbqk, sbv, icl, gate, kk, zr, sc, dd, dT, asT, ysb, vtok, bktok, sbt, smid, sfac,
         s1) = place(
            at, ("rkv", [12, TOK], F32), ("lw", [2, TOK], F32), ("sbqk", [8, TOK], F32),
            ("sbv", [TT, RW], F32), ("icl", [G, TOK], F32), ("gate", [G, TOK], F32),
            ("kk", [G, TOK], F32), ("zr", [G, 2, 2, P], F32), ("sc", [2, 4, 512], F32),
            ("dd", [2, 4, P], F32), ("dT", [2, 4, P], F32), ("asT", [2, 4, P], F32),
            ("ysb", [2, 4, P], F32), ("vtok", [TT, RW], F32), ("bktok", [2, RW], F32),
            ("sbt", [2, 384], F32), ("smid", [G, 2], F32), ("sfac", [G], F32), ("s1", [2, HD], F32))
        wsb, usb = place(starts["ysb"], ("wsb", [2, 4, HD], F32), ("usb", [2, 4, HD], F32))
        scr = sc[:].rearrange("p a b c -> p (a b c)").rearrange("p (t h n) -> p t h n", t=TT, h=4)
        sq2 = sc[:].rearrange("p a b c -> p (a b c)")[:, 0:KD * TOK]
        assert top[0] <= nc.sbuf_usable_end, (top[0], nc.sbuf_usable_end)
        rows, cols, coef = [rows0, rows1], [cols0, cols1], [coef0, coef1]

        def L(name, l):
            return a[f"{name}_{l}"]

        def width(l):
            return 3 * RW + LO_WA + LO_G + RANK * l

        def low_m(l, b):
            return LO_WA if b == 12 else LO_G + RANK * l

        def vtile(l, g):
            return vf[:, g] if l == 0 else rkv[:, 8 + g]

        def xn_half(t, half):
            return xn[:, t, half * 512:(half + 1) * 512]

        def x_half(t, half):
            return x[:, t, half * 512:(half + 1) * 512]

        def post_src(m, t, half):
            if m in (0, 2):
                return bank[half * 2 + t][:]
            if m == 1:
                return bank[4 + 2 * t + half][:]
            return acc[:, t, half * 512:(half + 1) * 512]

        def post_tmp(m, t, half):
            return scr[:, t, half] if m in (0, 2) else xn_half(t, half)

        ff, moe = Stream(s, "ff_", 2, 1, 0), Stream(s, "moe_", 1, 0, 1)

        def moe_tiles(eng, tiles, i):
            tiles(moe, i * NF, i * (NF // 2), i * NF, 0)
            tiles(moe, i * NF + 2, i * (NF // 2) + 1, i * NF + 2, 2)
            with eng.Fori(2, NF // 2) as j:
                tiles(moe, i * NF + 2 * j, i * (NF // 2) + j, i * NF + 2 * j, 4)

        def pair_no(l, pair):
            return l * 2 + pair

        def merge_no(l, pair, level, r):
            return (pair_no(l, pair) * (LEVELS - 1) + level - 1) * 2 + r

        block = ctx.enter_context(nc.Block())

        def group_used(eng, l, j):
            if j < 7:
                eng.wait_ge(s["proj_mm"], 24 * l + (4, 8, 12, 14, 18, 22, 24)[j])
            else:
                eng.wait_ge(s["wo_mm"], 4 * l + 2 * (j - 6))

        @block.sync
        def _(sp):
            def mixer_loads(l):
                for j in range(9):
                    q = 9 * l + j
                    if j >= 2:
                        group_used(sp, l, j - 2)
                    elif l == 1:
                        sp.wait_ge(s["ff_gu_lo"], 2 * (NF - 1 + j))
                    if j < 3:
                        src = L("w_in", l)[:, j * RW:(j + 1) * RW]
                    elif j == 3:
                        src = L("w_in", l)[:, 3 * RW:width(l)]
                    elif j < 7:
                        src = L("w_in", l)[:, width(l) + (j - 4) * RW:width(l) + (j - 3) * RW]
                    else:
                        src = L("w_out", l)[:, (j - 7) * RW:(j - 6) * RW]
                    sp.dma_start(raw_gu[:, q % 2, :, 0:src.shape[1]],
                                 src.rearrange("(k p) n -> p k n", p=P)).then_inc(mw_loaded[q % 2], 16)

            def load_gu(q, slot, wg, wu, f):
                for n, w in enumerate((wg, wu)):
                    sp.dma_start(raw_gu[:, slot, :, n * FT:(n + 1) * FT],
                                 w.rearrange("(k p) n -> p k n", p=P)[:, :, bass.ds(f * FT, FT)]
                                 ).then_inc(q.gu_loaded[slot], 16)

            def load_d(q, slot, wd, f):
                sp.dma_start(raw_d[:, slot], wd[bass.ds(f * FT, FT), :].rearrange("(c p) n -> p c n", p=P)
                             ).then_inc(q.d_loaded[slot], 16)

            mixer_loads(0)

            def slot_ff(f):
                return (f + ff.slot0) % 2

            dense = [L("ff_gate", 0), L("ff_up", 0), L("ff_down", 0)]
            for f in range(2):
                group_used(sp, 0, 7 + f)
                load_gu(ff, slot_ff(f), dense[0], dense[1], f)
            sp.wait_ge(s["bkzr_done"], 1)
            load_d(ff, slot_ff(0), dense[2], 0)
            for f in range(2, 4):
                sp.wait_ge(s["ff_gu_lo"], 2 * (f - 1))
                load_gu(ff, slot_ff(f), dense[0], dense[1], f)
                if f > 2:
                    sp.wait_ge(s["ff_d_lo"], f - 2)
                load_d(ff, slot_ff(f - 1), dense[2], f - 1)
            with sp.Fori(2, NF // 2) as j:
                for v in range(2):
                    sp.wait_ge(s["ff_gu_lo"], 4 * j + 2 * v - 2)
                    load_gu(ff, slot_ff(v), dense[0], dense[1], 2 * j + v)
                    sp.wait_ge(s["ff_d_lo"], 2 * j + v - 2)
                    load_d(ff, slot_ff(v + 1), dense[2], 2 * j + v - 1)
            sp.wait_ge(s["ff_d_lo"], NF - 2)
            load_d(ff, slot_ff(NF - 1), dense[2], NF - 1)

            mixer_loads(1)
            group_used(sp, 1, 7)
            first = [a["moe_gate_1"][0], a["moe_up_1"][0], a["moe_down_1"][0]]
            load_gu(moe, 0, first[0], first[1], 0)
            group_used(sp, 1, 8)
            load_gu(moe, 1, first[0], first[1], 1)
            sp.wait_ge(s["bkzr_done"], 2)
            load_d(moe, 0, first[2], 0)

            sp.wait_ge(s["table_ready"], 1)
            n_items = sp.value_load(table[0:1, 12:13], min_val=NE, max_val=MAX_ITEMS)

            def expert(i):
                e = sp.value_load(table[0:1, bass.ds(i, 1)], min_val=0, max_val=NE - 1)
                return [a[n][bass.ds(e, 1)].rearrange("o d f -> (o d) f")
                        for n in ("moe_gate_1", "moe_up_1", "moe_down_1")]

            with sp.Fori(0, n_items) as i:
                here = expert(i)
                with sp.Fori(0, NF // 2 - 1) as j:
                    for v in range(2):
                        sp.wait_ge(s["moe_gu_lo"], i * (2 * NF) + 4 * j + 2 * v + 2)
                        load_gu(moe, v, here[0], here[1], 2 * j + v + 2)
                        sp.wait_ge(s["moe_d_lo"], i * NF + 2 * j + v + 1)
                        load_d(moe, 1 - v, here[2], 2 * j + v + 1)
                following = expert(i + 1)
                sp.wait_ge(s["moe_gu_lo"], i * (2 * NF) + 2 * NF - 2)
                load_gu(moe, 0, following[0], following[1], 0)
                sp.wait_ge(s["moe_d_lo"], i * NF + NF - 1)
                load_d(moe, 1, here[2], NF - 1)
                sp.wait_ge(s["moe_gu_lo"], i * (2 * NF) + 2 * NF)
                load_gu(moe, 1, following[0], following[1], 1)
                sp.wait_ge(s["moe_d_lo"], i * NF + NF)
                load_d(moe, 0, following[2], 0)
            for v in range(2):
                sp.wait_ge(moe.gu_loaded[v], n_items * (16 * NF) + 32)
            sp.wait_ge(moe.d_loaded[0], n_items * (8 * NF) + 16)

            for t in range(TT):
                sp.wait_ge(s["x_ready"], 7 + t)
                sp.dma_start(out[0].rearrange("(t p) d -> p t d", p=P)[:, t], x[:, t]
                             ).then_inc(s["out_done"], 16)
            sp.wait_ge(s["out_done"], 32)

        @block.gpsimd
        def _(pool):
            step = [0]

            def link(ins):
                step[0] += 1
                ins.then_inc(s["pool_step"], 1)
                pool.wait_ge(s["pool_step"], step[0])

            def keep_where(out_ap, pattern, base, mult, compare=ALU.is_ge, fill=0.0):
                link(nc.gpsimd.affine_select(out=out_ap, in_=out_ap, compare_op=compare, fill=fill,
                                             base=base, pattern=pattern, channel_multiplier=mult))

            for l in range(2):
                nc.gpsimd.memset(rows[l][:], 0.0).then_inc(s["zeroed"], 1)

            def zero_ups():
                for w in (up_dec, up_icl, up_gate, up_vres):
                    last = nc.gpsimd.memset(w[:], 0.0)
                last.then_inc(s["ups_zero"], 1)

            zero_ups()
            nc.gpsimd.memset(ones[:], 1.0)
            nc.gpsimd.memset(neg_ones[:], -1.0)
            nc.gpsimd.memset(heads1[:], 0.0)
            nc.gpsimd.memset(heads64[:], 0.0)
            nc.gpsimd.memset(ident[:], 0.0)
            nc.gpsimd.memset(up_mask[:], 1.0)
            nc.gpsimd.memset(neg_low[:], -1.0)
            nc.gpsimd.memset(eps[:, 0:1], LNX_EPS)
            nc.gpsimd.memset(eps[:, 1:2], NORM_EPS)
            nc.gpsimd.memset(neg_mask[:], 0.0)
            nc.gpsimd.memset(level1[:], 0.0)
            link(nc.gpsimd.memset(levelT[:], 0.0))
            for hh in range(2):
                nc.gpsimd.memset(heads1[hh * HD:(hh + 1) * HD, hh * HD:(hh + 1) * HD], 1.0)
                link(nc.gpsimd.memset(heads64[hh * HD:(hh + 1) * HD, hh * HD:(hh + 1) * HD], 1.0 / HD))
            keep_where(ident[:], [[-1, P]], 0, 1, ALU.not_equal, 1.0)
            keep_where(up_mask[:, 0], [[1, P]], -1, -1)
            keep_where(up_mask[:, 1], [[1, P]], 0, -1)
            keep_where(neg_low[:], [[-1, P]], 0, 1)
            keep_where(neg_mask[:], [[1, P]], -1, -1, fill=MASKED)
            link(nc.gpsimd.memset(level1[:].rearrange("p (b h) -> p b h", h=2)[:, :, 0], 1.0))
            v1 = level1[:].rearrange("p (b h) -> p b h", h=2)[:, :, 0]
            keep_where(v1, [[-2, P // 2]], -1, 1)
            keep_where(v1, [[2, P // 2]], 1, -1)
            for n in range(LEVELS):
                size = 2 ** n
                v = levelT[:, n].rearrange("p (b h c) -> p b h c", h=2, c=size)[:, :, 1]
                link(nc.gpsimd.memset(v, 1.0))
                keep_where(v, [[-2 * size, P // (2 * size)], [0, size]], 0, 1)
                keep_where(v, [[2 * size, P // (2 * size)], [0, size]], size - 1, -1)
            nc.gpsimd.memset(heads1[0:1, 0:1], 1.0).then_inc(s["consts"], 1)

            def load_ups(l):
                pool.dma_start(up_dec[0:RANK], L("decay_up", l)).then_inc(s["ups_loaded"], 16)
                pool.dma_start(up_icl[RANK:2 * RANK], L("iclr_up", l)).then_inc(s["ups_loaded"], 16)
                pool.dma_start(up_gate[0:LO_G], L("gate_up", l)).then_inc(s["ups_loaded"], 16)
                if l:
                    pool.dma_start(up_vres[LO_G:P], L("vres_up", l)).then_inc(s["ups_loaded"], 16)

            def load_post(m):
                if m:
                    pool.wait_ge(s["x_ready"], 2 * m)
                g = L(["mix_post", "ffn_post"][m % 2], m // 2)
                pool.dma_start(gpost[:], g.partition_broadcast(P)).then_inc(s["post_loaded"], 16)

            def merges(l):
                for pair in range(2):
                    for level in range(1, LEVELS):
                        for r in range(2):
                            n = merge_no(l, pair, level, r)
                            if level == 1:
                                pool.wait_ge(s["score_ready"], l * G + 2 * pair + r + 1)
                            elif n >= 2:
                                pool.wait_ge(s["y_mm"], n - 1)
                            nc.gpsimd.tensor_tensor(
                                asT[:, r], sc[:, r, :, 0:P],
                                levelT[:, level:level + 1].to_broadcast([P, 4, P]), ALU.mult
                            ).then_inc(s["asT_done"], 1)

            pool.wait_ge(s["ups_zero"], 1)
            load_ups(0)
            load_post(0)
            pool.dma_start(router[:], a["router_1"].rearrange("(k p) e -> p k e", p=P)
                           ).then_inc(s["router_loaded"], 16)
            merges(0)
            load_post(1)
            pool.wait_ge(s["ff_dn_mm"], 2 * NF)
            pool.wait_ge(s["ff_hT_lo"], 2 * NF)
            zero_ups()
            pool.wait_ge(s["ups_zero"], 2)
            load_ups(1)
            load_post(2)
            pool.wait_ge(s["shifted"], 14 + 12)
            pool.wait_ge(s["gate_done"], 2 * G)
            v1 = rkv[:, 8:12]
            link(nc.gpsimd.tensor_tensor(vdiff[:], vf[:], v1, ALU.subtract))
            link(nc.gpsimd.tensor_tensor(vdiff[:], vdiff[:], vr[:], ALU.mult))
            nc.gpsimd.tensor_tensor(v1, v1, vdiff[:], ALU.add).then_inc(s["v_ready"], 1)
            pool.wait_ge(s["v_ready"], 1)
            pool.dma_start(gpre[:], L("ffn_pre", 1).partition_broadcast(P)).then_inc(s["gpre_loaded"], 16)
            merges(1)
            load_post(3)

        @block.scalar
        def _(act):
            step = [0]

            def link(ins):
                step[0] += 1
                ins.then_inc(s["act_step"], 1)
                act.wait_ge(s["act_step"], step[0])

            act.dma_start(x[:], a["x"][0].rearrange("(t p) d -> p t d", p=P)).then_inc(s["x_loaded"], 16)
            for l in range(2):
                act.wait_ge(s["zeroed"], l + 1)
                nl = width(l) - 3 * RW - LO_WA

                def row(name, count, ap):
                    act.dma_start(rows[l][ROW[name]:ROW[name] + count], ap).then_inc(s["params_loaded"], 16)
                row("mu", 12, L("mu", l)[0:3 * RW].rearrange("(r p) -> r p", p=P))
                act.dma_start(rows[l][12:13, 0:LO_WA], L("mu", l)[3 * RW:3 * RW + LO_WA].unsqueeze(0)
                              ).then_inc(s["params_loaded"], 16)
                act.dma_start(rows[l][13:14, 0:nl], L("mu", l)[3 * RW + LO_WA:width(l)].unsqueeze(0)
                              ).then_inc(s["params_loaded"], 16)
                for name in ("decay0", "iclr0", "k_k", "k_a", "lnx_g", "lnx_b", "sb_g") + ("vres0",) * l:
                    row(name, G, L(name, l).rearrange("(r p) -> r p", p=P))
                row("r_k", G, L("r_k", l).rearrange("(r q) p -> r (q p)", q=2))
                row("mix_pre", KD, L("mix_pre", l).rearrange("(r p) -> r p", p=P))
                row("ffn_pre", KD, L("ffn_pre", l).rearrange("(r p) -> r p", p=P))
            for l in range(2):
                act.wait_ge(s["cols_mm"], l + 1)
                nc.scalar.copy(cols[l][:], bank[6 + l][:, 0:NROWS]).then_inc(s["cols_ready"], 1)

            def norm(n):
                if n == 0:
                    act.wait_ge(s["x_loaded"], 16)
                for t in range(TT):
                    if n:
                        act.wait_ge(s["x_ready"], 2 * (n - 1) + t + 1)
                    nc.scalar.activation(xn[:, t], x[:, t], ACT.Square, accum_out=ss[:, t:t + 1]
                                         ).then_inc(s["sq_done"], 1)
                act.wait_ge(s["ms_done"], n + 1)
                link(nc.scalar.activation(rstd[:], ms[:], ACT.Ln))
                nc.scalar.activation(rstd[:], rstd[:], ACT.Exp, scale=-0.5).then_inc(s["rstd_done"], 1)
                l, gain = n // 2, ROW["ffn_pre" if n % 2 else "mix_pre"]
                act.wait_ge(s["cols_ready"], 2)
                for k in range(KD):
                    if n != 1 and k // 2 % 2:
                        continue
                    act.wait_ge(s["xT_mm"], 4 * n + k // 2 + 1)
                    src = bank[k // 2][:, (k % 2) * TOK:(k % 2 + 1) * TOK]
                    dst = xT_hi[:, k] if n == 1 else xnT[:, k]
                    nc.scalar.activation(dst, src, ACT.Copy, scale=cols[l][:, gain + k:gain + k + 1]
                                         ).then_inc(s["xT_act"], 1)

            def mixer(l):
                def block_bank(b, m=P, n=TOK):
                    return bank[4 + b % 4][0:m, 0:n]

                def shift(b):
                    act.wait_ge(s["proj_mm"], 24 * l + b + 1)
                    m = P if b < 12 else low_m(l, b)
                    dst = rkv[:, b] if b < 8 else vtile(l, b - 8) if b < 12 else lw[0:m, b - 12]
                    nc.scalar.activation(dst, block_bank(b, m), ACT.Copy, scale=coef[l][0:m, b:b + 1]
                                         ).then_inc(s["shift_act"], 1)

                def copy(b):
                    act.wait_ge(s["proj_mm"], 24 * l + b + 1)
                    if b < 22:
                        nc.scalar.activation(sbqk[:, b - 14], block_bank(b), ACT.Copy,
                                             scale=HD ** -0.5 if b < 18 else 1.0
                                             ).then_inc(s["sb_copied"], 1)
                    else:
                        nc.scalar.copy(sbv[:, b - 22], block_bank(b, n=512)).then_inc(s["sb_copied"], 1)

                act.wait_ge(s["coef_ready"], 2)
                for b in range(14):
                    shift(b)
                act.wait_ge(s["shifted"], 14 * l + 13)
                nc.scalar.activation(lw[0:RANK, 0], lw[0:RANK, 0], ACT.Tanh).then_inc(s["lw_ready"], 1)
                act.wait_ge(s["shifted"], 14 * l + 14)
                nc.scalar.activation(lw[0:LO_G, 1], lw[0:LO_G, 1], ACT.Sigmoid).then_inc(s["lw_ready"], 1)
                for b in range(14, 18):
                    copy(b)
                for g in range(G):
                    act.wait_ge(s["upA_mm"], l * G + g + 1)
                    d0, i0 = ROW["decay0"] + g, ROW["iclr0"] + g
                    nc.scalar.activation(sig[:, g], bank[g][:, 0:TOK], ACT.Sigmoid,
                                         bias=cols[l][:, d0:d0 + 1])
                    nc.scalar.activation(icl[:, g], bank[g][:, TOK:2 * TOK], ACT.Sigmoid,
                                         bias=cols[l][:, i0:i0 + 1]).then_inc(s["dec_done"], 1)
                for b in range(18, 24):
                    copy(b)
                for g in range(G):
                    act.wait_ge(s["upB_mm"], l * G + g + 1)
                    if l:
                        v0 = ROW["vres0"] + g
                        nc.scalar.activation(vr[:, g], bank[g][:, TOK:2 * TOK], ACT.Sigmoid,
                                             bias=cols[l][:, v0:v0 + 1])
                    nc.scalar.copy(gate[:, g], bank[g][:, 0:TOK]).then_inc(s["gate_done"], 1)
                act.wait_ge(s["kkr_done"], l + 1)
                nc.scalar.activation(rn[:], kk[:], ACT.Square).then_inc(s["kksq_done"], 1)
                act.wait_ge(s["cd_done"], l + 1)
                nc.scalar.activation(pdec[:], cum[:], ACT.Exp, scale=-DECAY_SCALE)
                link(nc.scalar.activation(sfac[:], smid[:, :, 1], ACT.Exp, scale=-DECAY_SCALE))
                nc.scalar.activation(cum[:], cum[:], ACT.Exp, scale=DECAY_SCALE)
                nc.scalar.activation(sig[:], sig[:], ACT.Exp, scale=-DECAY_SCALE
                                     ).then_inc(s["decays_done"], 1)
                act.wait_ge(s["nn_done"], l + 1)
                link(nc.scalar.activation(rn[:], rn[:], ACT.Ln))
                nc.scalar.activation(rn[:], rn[:], ACT.Exp, scale=-0.5).then_inc(s["rn_done"], 1)
                for i, dst in enumerate((vtok[:, 0], vtok[:, 1], bktok[:, 0], bktok[:, 1])):
                    act.wait_ge(s["tok_mm"], 4 * l + i + 1)
                    nc.scalar.copy(dst, bank[(6, 7, 4, 5)[i]][:]).then_inc(s["tok_ready"], 1)

                def sb_softplus(hd):
                    z, buf = bank[6 + hd % 2][:, 0:384], sbt[:, hd % 2]
                    act.wait_ge(s["z_mm"], l * NSB + hd + 1)
                    link(nc.scalar.activation(buf, z, ACT.Abs))
                    link(nc.scalar.activation(buf, buf, ACT.Exp, scale=-1.0))
                    nc.scalar.activation(buf, buf, ACT.Ln, bias=ones[:, 0:1]).then_inc(s["softplus_ln"], 1)

                def sb_exp(hd):
                    act.wait_ge(s["arg_done"], l * NSB + hd + 1)
                    nc.scalar.activation(sbt[:, hd % 2], sbt[:, hd % 2], ACT.Exp).then_inc(s["att_exp"], 1)

                def sb_out(hd):
                    act.wait_ge(s["o_mm"], l * NSB + hd + 1)
                    rowsl = slice((hd % 2) * HD, (hd % 2 + 1) * HD)
                    nc.scalar.copy(yo[rowsl, G + hd // 2], bank[6 + hd % 2][rowsl, 0:TOK]
                                   ).then_inc(s["o_copied"], 1)

                for pair in range(2):
                    for level in range(1, LEVELS):
                        slot = pair * (LEVELS - 1) + level - 1
                        for r in range(2):
                            n = merge_no(l, pair, level, r)
                            act.wait_ge(s["y_mm"], n + 1)
                            nc.scalar.copy(ysb[:, r], bank[3 * r][:]).then_inc(s["y_copied"], 1)
                        if 0 <= slot - 2 < NSB:
                            sb_out(slot - 2)
                        if slot < NSB:
                            sb_softplus(slot)
                        if 0 <= slot - 1 < NSB:
                            sb_exp(slot - 1)
                    base = pair_no(l, pair)
                    four = lambda b: bank[b][:, 0:4 * HD].rearrange("p (q v) -> p q v", v=HD)
                    act.wait_ge(s["solve_mm"], 6 * base + 1)
                    nc.scalar.copy(wsb[:, 0], four(0)).then_inc(s["solve_act"], 1)
                    act.wait_ge(s["solve_mm"], 6 * base + 2)
                    nc.scalar.copy(usb[:, 0], four(1)).then_inc(s["solve_act"], 1)
                    act.wait_ge(s["solve_mm"], 6 * base + 4)
                    for hh in range(2):
                        w1 = wsb[:, 1].rearrange("p (r h) v -> p r h v", h=2)[:, :, hh]
                        last = nc.scalar.copy(w1, bank[4 + hh][:, 0:2 * HD].rearrange(
                            "p (r v) -> p r v", v=HD))
                    last.then_inc(s["solve_act"], 1)
                    act.wait_ge(s["solve_mm"], 6 * base + 5)
                    nc.scalar.copy(usb[:, 1], four(0)).then_inc(s["solve_act"], 1)
                    act.wait_ge(s["solve_mm"], 6 * base + 6)
                    nc.scalar.copy(yo[0:HD, 2 * pair:2 * pair + 2],
                                   bank[1][0:HD].rearrange("p (g n) -> p g n", g=2)).then_inc(s["yT_act"], 1)

                act.wait_ge(s["centred"], 2 * (l + 1))
                act.wait_ge(s["yT_act"], 2 * (l + 1))
                act.wait_ge(s["o_copied"], NSB * (l + 1))
                nc.scalar.activation(sq2, yo[:].rearrange("p k n -> p (k n)"), ACT.Square
                                     ).then_inc(s["sq2_done"], 1)
                for i in range(4):
                    act.wait_ge(s["var_mm"], 4 * l + i + 1)
                    dst = sq2[:, i * 512:(i + 1) * 512]
                    e = int(i >= 2)
                    link(nc.scalar.activation(dst, bank[2 + i][:], ACT.Ln, bias=eps[:, e:e + 1]))
                    nc.scalar.activation(dst, dst, ACT.Exp, scale=-0.5).then_inc(s["rs_done"], 1)

            def post(m):
                for t in range(TT):
                    for half in range(2):
                        if m in (0, 2):
                            act.wait_ge(s["wo_mm"], 4 * (m // 2) + half * 2 + t + 1)
                        nc.scalar.activation(post_tmp(m, t, half), post_src(m, t, half), ACT.Square,
                                             accum_out=pss[:, t, half:half + 1]).then_inc(s["post_sq"], 1)
                act.wait_ge(s["post_ms"], m + 1)
                link(nc.scalar.activation(rstd[:], ms[:], ACT.Ln))
                nc.scalar.activation(rstd[:], rstd[:], ACT.Exp, scale=-0.5).then_inc(s["post_rstd"], 1)

            def split_gu(q, slot, tile, load, first=False):
                act.wait_ge(q.gu_loaded[slot], load * 32)
                if not first:
                    act.wait_ge(q.gu_mm, tile * q.T - q.T)
                for piece in range(2):
                    k = slice(piece * KD // 2, (piece + 1) * KD // 2)
                    nc.scalar.copy(gu_hi[:, slot, k], raw_gu[:, slot, k]).then_inc(q.gu_hi, 1)

            def split_d(q, slot, tile, load, first=False):
                act.wait_ge(q.d_loaded[slot], load * 16)
                if not first:
                    act.wait_ge(q.dn_mm, tile * q.T - q.T)
                nc.scalar.copy(d_hi[:, slot], raw_d[:, slot]).then_inc(q.d_hi, 1)

            def silu_of(q, u, v):
                act.wait_ge(q.gu_mm, u + 1)
                nc.scalar.activation(silu[:, v], bank[v][:, 0:FT], ACT.Silu).then_inc(q.silu, 1)

            def hT_of(q, u, v):
                act.wait_ge(q.tr_mm, u + 1)
                nc.scalar.copy(hT_hi[:, v], bank[2 + v][:, 0:2 * P].rearrange("p (c n) -> p c n", n=P)
                               ).then_inc(q.hT_hi, 1)

            def tiles(q, f0, load0, u0, local, next_split=True):
                for w in range(2):
                    slot, nxt = (w + q.slot0) % 2, (w + 1 + q.slot0) % 2
                    if next_split or w == 0:
                        split_gu(q, nxt, f0 + w + 1, load0 + 1 + w, first=local + w == 0)
                    for t in range(q.T):
                        v = (w * q.T + t) % 2
                        u = u0 + w * q.T + t
                        silu_of(q, u, v)
                        if not (local == 0 and w == 0 and t == 0):
                            hT_of(q, u - 1, 1 - v)
                    split_d(q, slot, f0 + w, load0 + 1, first=local + w < 2)

            norm(0)
            mixer(0)
            post(0)
            norm(1)
            act.wait_ge(s["x_ready"], 2)
            split_gu(ff, ff.slot0, 0, 1, first=True)
            tiles(ff, 0, 0, 0, 0)
            with act.Fori(1, NF // 2 - 1) as j:
                tiles(ff, 2 * j, j, 4 * j, 2)
            tiles(ff, NF - 2, NF // 2 - 1, 2 * NF - 4, 2, next_split=False)
            hT_of(ff, 2 * NF - 1, 1)
            act.wait_ge(s["ff_dn_mm"], 2 * NF)
            post(1)
            norm(2)
            mixer(1)
            post(2)
            norm(3)
            act.wait_ge(s["picks_done"], 1)
            nc.scalar.activation(route[:, 8, 0:2], route[:, 8, 0:2], ACT.Exp).then_inc(s["gates_exp"], 1)
            act.wait_ge(s["mixed"], 16)
            act.wait_ge(s["wo_mm"], 8)
            split_gu(moe, 0, 0, 1, first=True)
            act.wait_ge(s["table_ready"], 1)
            n_items = act.value_load(table[0:1, 12:13], min_val=NE, max_val=MAX_ITEMS)
            with act.Fori(0, n_items) as i:
                for b in range(2):
                    act.wait_ge(s["gather_mm"], i * 2 + b + 1)
                    nc.scalar.copy(xT_hi[:, 4 * b:4 * b + 4, 0:P],
                                   bank[6 + b][:].rearrange("p (k n) -> p k n", n=P)).then_inc(s["xg_hi"], 1)
                act.wait_ge(s["sel_t_mm"], i + 1)
                nc.scalar.copy(selT[:], bank[2][:, 0:TOK].rearrange("p (t n) -> p t n", n=P)
                               ).then_inc(s["sel_t_done"], 1)
                moe_tiles(act, tiles, i)
                hT_of(moe, i * NF + NF - 1, 1)
                act.wait_ge(s["moe_dn_mm"], i * NF + NF)
                for half in range(2):
                    nc.scalar.copy(y_sb[:, half * 512:(half + 1) * 512], bank[4 + half][:]
                                   ).then_inc(s["y_evicted"], 1)
            act.wait_ge(s["acc_added"], n_items * 4 + 4)
            post(3)

        @block.vector
        def _(dve):
            step = [0]

            def link(ins):
                step[0] += 1
                ins.then_inc(s["dve_step"], 1)
                dve.wait_ge(s["dve_step"], step[0])

            TTop, TSop, STT = nc.vector.tensor_tensor, nc.vector.tensor_scalar, nc.vector.scalar_tensor_tensor

            dve.wait_ge(s["consts"], 1)
            link(nc.vector.tensor_tensor_scan(iota1[:], ones[:], ones[:], 0.0, ALU.mult, ALU.add))
            for l in range(2):
                dve.wait_ge(s["cols_ready"], l + 1)
                c = ROW["k_a"]
                TSop(coef[l][:, 0:14], cols[l][:, 0:14], -1.0, 1.0, ALU.mult, ALU.add)
                TSop(coef[l][:, 14:18], cols[l][:, c:c + G], -1.0, 1.0, ALU.mult, ALU.add
                     ).then_inc(s["coef_ready"], 1)

            def norm(n):
                dve.wait_ge(s["sq_done"], 2 * n + 2)
                TSop(ms[:], ss[:], 1.0 / D, NORM_EPS, ALU.mult, ALU.add).then_inc(s["ms_done"], 1)
                dve.wait_ge(s["rstd_done"], n + 1)
                for t in range(TT):
                    TSop(xn[:, t], x[:, t], rstd[:, t:t + 1], None, ALU.mult).then_inc(s["xn_ready"], 1)
                l, gain = n // 2, ROW["ffn_pre" if n % 2 else "mix_pre"]
                for k in range(KD):
                    if n != 1 and k // 2 % 2 == 0:
                        continue
                    dve.wait_ge(s["xT_mm"], 4 * n + k // 2 + 1)
                    src = bank[k // 2][:, (k % 2) * TOK:(k % 2 + 1) * TOK]
                    col = cols[l][:, gain + k:gain + k + 1]
                    if n == 1:
                        dve.wait_ge(s["xT_act"], 4 + 2 * (k // 2) + 2)
                        STT(xT_lo[:, k], src, col, xT_hi[:, k].bitcast(F32), ALU.mult, ALU.subtract
                            ).then_inc(s["xT_dve"], 1)
                    else:
                        TSop(xnT[:, k], src, col, None, ALU.mult).then_inc(s["xT_dve"], 1)

            def mixer(l):
                col = lambda name, g: cols[l][:, ROW[name] + g:ROW[name] + g + 1]
                for b in range(14):
                    m = P if b < 12 else low_m(l, b)
                    dst = rkv[:, b] if b < 8 else vtile(l, b - 8) if b < 12 else lw[0:m, b - 12]
                    dve.wait_ge(s["shift_act"], 14 * l + b + 1)
                    STT(dst[:, 1:TOK], bank[4 + b % 4][0:m, 0:TOK - 1], cols[l][0:m, b:b + 1],
                        dst[:, 1:TOK], ALU.mult, ALU.add).then_inc(s["shifted"], 1)
                dve.wait_ge(s["shifted"], 14 * l + 14)
                for g in range(G):
                    last = TSop(kk[:, g], rkv[:, 4 + g], col("k_k", g), None, ALU.mult)
                last.then_inc(s["kkr_done"], 1)
                for g in range(G):
                    dve.wait_ge(s["dec_done"], l * G + g + 1)
                    for c in range(2):
                        tok = slice(c * P, (c + 1) * P)
                        last = nc.vector.tensor_tensor_scan(cum[:, g, tok], ones[:], sig[:, g, tok], 0.0,
                                                            ALU.mult, ALU.add)
                link(last)
                cum4 = cum[:].rearrange("p g (c n) -> p g c n", c=2)
                link(nc.vector.tensor_copy(smid[:], cum4[:, :, :, MID]))
                for g in range(G):
                    for c in range(2):
                        tok = slice(c * P, (c + 1) * P)
                        last = TSop(cum[:, g, tok], cum[:, g, tok], smid[:, g, c:c + 1], None, ALU.subtract)
                link(last)
                TTop(sig[:], cum[:], sig[:], ALU.subtract).then_inc(s["cd_done"], 1)
                for g in range(G):
                    link(TSop(vscr(g), icl[:, g], col("k_a", g), coef[l][:, 14 + g:15 + g], ALU.mult,
                              ALU.add))
                    last = TTop(rkv[:, 4 + g], rkv[:, 4 + g], vscr(g), ALU.mult)
                link(last)
                dve.wait_ge(s["kkn_mm"], l + 1)
                for i in range(2):
                    last = TSop(rn[:, 2 * i:2 * i + 2], bank[4 + i][:].rearrange("p (g n) -> p g n", g=2),
                                1e-12, None, ALU.max)
                last.then_inc(s["nn_done"], 1)
                dve.wait_ge(s["rn_done"], l + 1)
                link(TTop(kk[:], kk[:], rn[:], ALU.mult))
                dve.wait_ge(s["decays_done"], l + 1)
                zr8 = zr[:].rearrange("p g c z n -> p (g c) z n")
                fold = lambda ap: ap.rearrange("p g (c n) -> p (g c) n", c=2)
                TTop(sfac[:], sfac[:], pdec[:, :, P - 1], ALU.mult)
                STT(zr8[:, :, 0], fold(kk[:]), -1.0, fold(sig[:]), ALU.mult, ALU.mult)
                link(TTop(icl[:], icl[:], kk[:], ALU.mult))
                TTop(icl[:], icl[:], cum[:], ALU.mult)
                link(TTop(zr8[:, :, 1], fold(rkv[:, 0:4]), fold(pdec[:]), ALU.mult))
                for g in range(G):
                    last = STT(rkv[:, g], rkv[:, g], col("r_k", g), rkv[:, 4 + g], ALU.mult, ALU.mult)
                last.then_inc(s["rr_done"], 1)
                dve.wait_ge(s["rr_done"], l + 1)
                TTop(rkv[:, 4:8], rkv[:, 4:8], cum[:], ALU.mult).then_inc(s["bkzr_done"], 1)
                dve.wait_ge(s["bonus_mm"], l + 1)
                if l:
                    dve.wait_ge(s["v_ready"], 1)
                vall = vf[:] if l == 0 else rkv[:, 8:12]
                for i in range(2):
                    last = TTop(rkv[:, 2 * i:2 * i + 2], vall[:, 2 * i:2 * i + 2],
                                bank[4 + i][:].rearrange("p (g n) -> p g n", g=2), ALU.mult)
                last.then_inc(s["bonus_done"], 1)

                def scores(g):
                    r = g % 2
                    dve.wait_ge(s["score_mm"], l * G + g + 1)
                    for p in range(4):
                        TTop(sc[:, r, p].rearrange("p (b n) -> p b n", b=2),
                             bank[p][:].rearrange("p (b n) -> p b n", b=2),
                             up_mask[:].rearrange("p z n -> p (z n)").unsqueeze(1).to_broadcast([P, 2, 2 * P]),
                             ALU.mult)
                    for hh in range(2):
                        link(TTop(dd[:, r, 2 * hh:2 * hh + 2],
                                  bank[4 + hh][:, 0:2 * P].rearrange("p (c n) -> p c n", c=2),
                                  level1[:].unsqueeze(1).to_broadcast([P, 2, P]), ALU.mult))
                    link(TTop(dT[:, r], sc[:, r, :, 0:P], levelT[:, 0:1].to_broadcast([P, 4, P]), ALU.mult))
                    ident4 = ident[:].unsqueeze(1).to_broadcast([P, 4, P])
                    TTop(dd[:, r], dd[:, r], ident4, ALU.add)
                    TTop(dT[:, r], dT[:, r], ident4, ALU.add).then_inc(s["score_ready"], 1)

                def sb_mask(hd):
                    z, buf = bank[6 + hd % 2][:, 0:384], sbt[:, hd % 2]
                    dve.wait_ge(s["softplus_ln"], l * NSB + hd + 1)
                    link(STT(buf, z, 0.0, buf, ALU.max, ALU.add))
                    diag = buf.rearrange("p (b n) -> p b n", n=P)[:, 0:3:2]
                    TTop(diag, diag, up_mask[:, 0:1].to_broadcast([P, 2, P]), ALU.mult
                         ).then_inc(s["spm_done"], 1)

                def sb_arg(hd):
                    z, buf = bank[6 + hd % 2][:, 0:384], sbt[:, hd % 2]
                    dve.wait_ge(s["arg_mm"], l * NSB + hd + 1)
                    link(TSop(buf, z, 0.0, None, ALU.min))
                    diag = buf.rearrange("p (b n) -> p b n", n=P)[:, 0:3:2]
                    TTop(diag, diag, neg_mask[:].unsqueeze(1).to_broadcast([P, 2, P]), ALU.add
                         ).then_inc(s["arg_done"], 1)

                for pair in range(2):
                    for r in range(2):
                        scores(2 * pair + r)
                    for level in range(1, LEVELS):
                        slot = pair * (LEVELS - 1) + level - 1
                        for r in range(2):
                            dve.wait_ge(s["g_mm"], merge_no(l, pair, level, r) + 1)
                            flat = lambda b: bank[b][:].rearrange("p (q n) -> p q n", n=P)
                            if level < LEVELS - 1:
                                TTop(dd[:, r], dd[:, r], flat(3 * r + 1), ALU.add)
                            TTop(dT[:, r], dT[:, r], flat(3 * r + 2), ALU.add).then_inc(s["d_ready"], 1)
                        if slot < NSB:
                            sb_mask(slot)
                        if 0 <= slot - 1 < NSB:
                            sb_arg(slot - 1)
                    base = pair_no(l, pair)
                    dve.wait_ge(s["solve_mm"], 6 * base + 3)
                    for hh in range(2):
                        ch = slice(hh * HD, (hh + 1) * HD)
                        for r in range(2):
                            g = 2 * pair + r
                            last = TSop(s1[ch, r], bank[2 + hh][ch, r * HD:(r + 1) * HD],
                                        sfac[ch, g:g + 1], None, ALU.mult)
                    last.then_inc(s["solve_dve"], 1)
                    dve.wait_ge(s["solve_mm"], 6 * base + 6)
                    nc.vector.tensor_copy(yo[HD:P, 2 * pair:2 * pair + 2],
                                          bank[2][HD:P].rearrange("p (g n) -> p g n", g=2)
                                          ).then_inc(s["yT_dve"], 1)
                for i in range(2):
                    dve.wait_ge(s["mean_mm"], 2 * l + i + 1)
                    y2 = yo[:, 2 * i:2 * i + 2]
                    TTop(y2, y2, bank[i][:].rearrange("p (g n) -> p g n", g=2), ALU.subtract
                         ).then_inc(s["centred"], 1)
                rs = sq2.rearrange("p (k n) -> p k n", n=TOK)
                for k in list(range(G, KD)) + list(range(G)):
                    dve.wait_ge(s["rs_done"], 4 * l + k // 2 + 1)
                    if k >= G:
                        STT(yo[:, k], yo[:, k], col("sb_g", k - G), rs[:, k], ALU.mult, ALU.mult
                            ).then_inc(s["mixed"], 1)
                    else:
                        dve.wait_ge(s["centred"], 2 * l + 2)
                        link(TTop(yo[:, k], yo[:, k], rs[:, k], ALU.mult))
                        link(TSop(yo[:, k], yo[:, k], col("lnx_g", k), col("lnx_b", k), ALU.mult, ALU.add))
                        link(TTop(yo[:, k], yo[:, k], rkv[:, k], ALU.add))
                        TTop(yo[:, k], yo[:, k], gate[:, k], ALU.mult).then_inc(s["mixed"], 1)

            def vscr(g):
                return dd[:].rearrange("p r q n -> p (r q n)")[:, g * TOK:(g + 1) * TOK]

            def post(m):
                dve.wait_ge(s["post_sq"], 4 * m + 4)
                link(TTop(ms[:], pss[:, :, 0], pss[:, :, 1], ALU.add))
                TSop(ms[:], ms[:], 1.0 / D, NORM_EPS, ALU.mult, ALU.add).then_inc(s["post_ms"], 1)
                dve.wait_ge(s["post_rstd"], m + 1)
                dve.wait_ge(s["post_loaded"], 16 * (m + 1))
                for t in range(TT):
                    for half in range(2):
                        link(STT(post_tmp(m, t, half), post_src(m, t, half), rstd[:, t:t + 1],
                                 gpost[:, half * 512:(half + 1) * 512], ALU.mult, ALU.mult))
                        last = TTop(x_half(t, half), x_half(t, half), post_tmp(m, t, half), ALU.add)
                    last.then_inc(s["x_ready"], 1)

            def split_gu(q, slot, tile, load, first=False):
                for piece in range(2):
                    dve.wait_ge(q.gu_hi, 2 * tile + piece + 1)
                    k = slice(piece * KD // 2, (piece + 1) * KD // 2)
                    TTop(gu_lo[:, slot, k], raw_gu[:, slot, k], gu_hi[:, slot, k].bitcast(F32), ALU.subtract
                         ).then_inc(q.gu_lo, 1)

            def split_d(q, slot, tile, load, first=False):
                dve.wait_ge(q.d_hi, tile + 1)
                TTop(d_lo[:, slot], raw_d[:, slot], d_hi[:, slot].bitcast(F32), ALU.subtract
                     ).then_inc(q.d_lo, 1)

            def h_of(q, u, v):
                dve.wait_ge(q.silu, u + 1)
                TTop(h[:, v], silu[:, v], bank[v][:, FT:2 * FT], ALU.mult).then_inc(q.h_done, 1)

            def hT_of(q, u, v):
                dve.wait_ge(q.hT_hi, u + 1)
                TTop(hT_lo[:, v], bank[2 + v][:, 0:2 * P].rearrange("p (c n) -> p c n", n=P),
                     hT_hi[:, v].bitcast(F32), ALU.subtract).then_inc(q.hT_lo, 1)

            def tiles(q, f0, load0, u0, local, next_split=True):
                for w in range(2):
                    slot, nxt = (w + q.slot0) % 2, (w + 1 + q.slot0) % 2
                    if next_split or w == 0:
                        split_gu(q, nxt, f0 + w + 1, None)
                    for t in range(q.T):
                        v = (w * q.T + t) % 2
                        u = u0 + w * q.T + t
                        h_of(q, u, v)
                        if not (local == 0 and w == 0 and t == 0):
                            hT_of(q, u - 1, 1 - v)
                    split_d(q, slot, f0 + w, None)

            norm(0)
            mixer(0)
            post(0)
            norm(1)
            split_gu(ff, ff.slot0, 0, None)
            tiles(ff, 0, 0, 0, 0)
            with dve.Fori(1, NF // 2 - 1) as j:
                tiles(ff, 2 * j, j, 4 * j, 2)
            tiles(ff, NF - 2, None, 2 * NF - 4, 2, next_split=False)
            hT_of(ff, 2 * NF - 1, 1)
            post(1)
            norm(2)
            mixer(1)
            post(2)
            norm(3)

            dve.wait_ge(s["gpre_loaded"], 16)
            dve.wait_ge(s["xT_mm"], 16)
            for t in range(TT):
                last = TTop(xn[:, t], xn[:, t], gpre[:], ALU.mult)
            last.then_inc(s["hn_ready"], 1)
            dve.wait_ge(s["router_mm"], 1)
            R = lambda i: route[:, i].rearrange("p (t e) -> p t e", t=TT)
            lg, eq, pick1, pick2, tmp, dense = R(0), R(1), R(2), R(3), R(4), R(5)
            picked = R(6)
            best = route[:, 7, 0:2]
            second = route[:, 7, 2:4]
            diff = route[:, 8, 0:2]
            g1, g2 = route[:, 9, 0:2], route[:, 9, 2:4]
            wide = lambda ap: ap.unsqueeze(2).to_broadcast([P, TT, NE])

            def choose(logits, top_of, pick):
                link(nc.vector.tensor_reduce(top_of, logits, AX.X, ALU.max))
                link(TTop(eq, logits, wide(top_of), ALU.is_equal))
                for t in range(TT):
                    link(nc.vector.tensor_tensor_scan(tmp[:, t], ones[:, 0:NE], eq[:, t], 0.0, ALU.mult,
                                                      ALU.add))
                link(TSop(tmp, tmp, 1.0, None, ALU.is_equal))
                link(TTop(pick, eq, tmp, ALU.mult))

            link(nc.vector.tensor_copy(lg, bank[6][:, 0:TT * NE].rearrange("p (t e) -> p t e", t=TT)))
            choose(lg, best, pick1)
            link(STT(lg, pick1, -3e38, lg, ALU.mult, ALU.add))
            choose(lg, second, pick2)
            link(TTop(picked, pick1, pick2, ALU.add))
            TTop(diff, second, best, ALU.subtract).then_inc(s["picks_done"], 1)
            dve.wait_ge(s["gates_exp"], 1)
            link(TSop(g1, diff, 1.0, None, ALU.add))
            link(nc.vector.reciprocal(g1, g1))
            link(TTop(g2, diff, g1, ALU.mult))
            link(TTop(dense, pick1, wide(g1), ALU.mult))
            link(TTop(tmp, pick2, wide(g2), ALU.mult))
            link(TTop(dense, dense, tmp, ALU.add))
            dve.wait_ge(s["counts_mm"], 1)
            pos = R(4)
            link(nc.vector.tensor_copy(pos, bank[7][:, 0:TT * NE].rearrange("p (t e) -> p t e", t=TT)))
            over, rank, one, val = (counts[:, i] for i in range(4))
            link(TSop(over, bank[7][:, 32:32 + NE], float(P), None, ALU.is_gt))
            link(nc.vector.tensor_tensor_scan(rank, ones[:, 0:NE], over, 0.0, ALU.mult, ALU.add))
            nc.vector.tensor_copy(item_pos[:, :, 0:NE], pos)
            nc.vector.tensor_copy(item_sel[:, :, 0:NE], picked)
            nc.vector.tensor_copy(item_gate[:, :, 0:NE], dense)
            for j in range(MAX_ITEMS - NE):
                link(TSop(one, rank, float(j + 1), None, ALU.is_equal))
                link(TTop(one, one, over, ALU.mult))
                link(TTop(val, one, iota1[:, 0:NE], ALU.mult))
                link(nc.vector.tensor_reduce(route[:, 7, 4 + j:5 + j], val, AX.X, ALU.add))
                for src, dst in ((pos, item_pos), (picked, item_sel), (dense, item_gate)):
                    link(TTop(eq, src, one.unsqueeze(1).to_broadcast([P, TT, NE]), ALU.mult))
                    link(nc.vector.tensor_reduce(dst[:, :, NE + j], eq, AX.X, ALU.add))
            link(TSop(item_pos[:, :, NE:MAX_ITEMS], item_pos[:, :, NE:MAX_ITEMS], -float(P), None, ALU.add))
            TSop(table[:, 0:NE], iota1[:, 0:NE], -1.0, None, ALU.add)
            nc.vector.memset(table[:, MAX_ITEMS:12], 0).then_inc(s["moe_d_lo"], 1)
            TSop(table[:, NE:MAX_ITEMS], route[:, 7, 4:4 + MAX_ITEMS - NE], -1.0, 0.0, ALU.add, ALU.max)
            TSop(table[:, 12:13], rank[:, NE - 1:NE], float(NE), None, ALU.add).then_inc(s["table_ready"], 1)
            dve.wait_ge(s["router_mm"], 1)
            nc.vector.memset(acc[:], 0.0).then_inc(s["acc_added"], 4)
            split_gu(moe, 0, 0, None)
            dve.wait_ge(s["table_ready"], 1)
            n_items = dve.value_load(table[0:1, 12:13], min_val=NE, max_val=MAX_ITEMS)
            with dve.Fori(0, n_items) as i:
                for t in range(TT):
                    at_i = bass.ds(i, 1)
                    TSop(sel[:, t], iota1[:], item_pos[:, t, at_i], item_sel[:, t, at_i], ALU.is_equal,
                         ALU.mult)
                    last = TSop(selg[:, t], iota1[:], item_pos[:, t, at_i], item_gate[:, t, at_i],
                                ALU.is_equal, ALU.mult)
                last.then_inc(s["sel_done"], 1)
                for b in range(2):
                    dve.wait_ge(s["xg_hi"], i * 2 + b + 1)
                    TTop(xg_lo[:, 4 * b:4 * b + 4], bank[6 + b][:].rearrange("p (k n) -> p k n", n=P),
                         xT_hi[:, 4 * b:4 * b + 4, 0:P].bitcast(F32), ALU.subtract).then_inc(s["xg_lo"], 1)
                moe_tiles(dve, tiles, i)
                hT_of(moe, i * NF + NF - 1, 1)
                for t in range(TT):
                    for half in range(2):
                        k = 2 * t + half
                        dve.wait_ge(s["scatter_mm"], i * 4 + k + 1)
                        dve.wait_ge(s["acc_added"], i * 4 + k + 1)
                        piece = acc[:, t, half * 512:(half + 1) * 512]
                        TTop(piece, piece, bank[(6, 7, 2, 3)[k]][:], ALU.add).then_inc(s["acc_added"], 1)
            post(3)

        @block.tensor
        def _(pe):
            mm = nc.tensor.matmul
            pe.wait_ge(s["consts"], 1)
            pe.wait_ge(s["params_loaded"], 16 * (13 + 14))
            for l in range(2):
                nc.tensor.transpose(bank[6 + l][:, 0:NROWS], rows[l][0:NROWS, :], ident[0:NROWS, 0:NROWS]
                                    ).then_inc(s["cols_mm"], 1)

            def norm(n):
                for t in range(TT):
                    pe.wait_ge(s["xn_ready"], 2 * n + t + 1)
                    for k in range(KD):
                        at_c = (k % 2) * TOK + t * P
                        last = nc.tensor.transpose(bank[k // 2][:, at_c:at_c + P],
                                                   xn[:, t, k * P:(k + 1) * P], ident[:])
                        if t and k % 2:
                            last.then_inc(s["xT_mm"], 1)

            def mixer(l):
                W = lambda j: raw_gu[:, (9 * l + j) % 2]

                def loaded(j):
                    q = 9 * l + j
                    pe.wait_ge(mw_loaded[q % 2], 16 * (q // 2 + 1))

                def project(b, j, c0, m):
                    if b >= 4:
                        if b - 4 < 14:
                            pe.wait_ge(s["shifted"], 14 * l + b - 3)
                        else:
                            pe.wait_ge(s["sb_copied"], 10 * l + b - 17)
                    for k in range(KD):
                        last = mm(bank[4 + b % 4][0:m, 0:TOK], W(j)[:, k, c0:c0 + m], xnT[:, k],
                                  start=k == 0, stop=k == KD - 1)
                    last.then_inc(s["proj_mm"], 1)
                    return last

                pe.wait_ge(s["xT_act"], [4, 16][l])
                pe.wait_ge(s["xT_dve"], [4, 16][l])
                b = 0
                for j in range(3):
                    loaded(j)
                    for i in range(4):
                        project(b, j, i * P, P)
                        b += 1
                loaded(3)
                project(12, 3, 0, LO_WA)
                project(13, 3, LO_WA, low_m(l, 13))
                loaded(4)
                for i in range(4):
                    project(14 + i, 4, i * P, P)
                pe.wait_ge(s["ups_loaded"], [48, 112][l])
                pe.wait_ge(s["lw_ready"], 2 * l + 1)
                for g in range(G):
                    ch = slice(g * P, (g + 1) * P)
                    mm(bank[g][:, 0:TOK], up_dec[0:LO_WA, ch], lw[0:LO_WA, 0], start=True, stop=True)
                    mm(bank[g][:, TOK:2 * TOK], up_icl[0:LO_WA, ch], lw[0:LO_WA, 0], start=True, stop=True
                       ).then_inc(s["upA_mm"], 1)
                loaded(5)
                for i in range(4):
                    project(18 + i, 5, i * P, P)
                loaded(6)
                for t in range(TT):
                    pe.wait_ge(s["sb_copied"], 10 * l + 22 + t - 17)
                    for k in range(KD):
                        last = mm(bank[4 + (22 + t) % 4][:], xnT[:, k, t * P:(t + 1) * P], W(6)[:, k],
                                  start=k == 0, stop=k == KD - 1)
                    last.then_inc(s["proj_mm"], 1)
                pe.wait_ge(s["lw_ready"], 2 * l + 2)
                mg = low_m(l, 13)
                for g in range(G):
                    pe.wait_ge(s["dec_done"], l * G + g + 1)
                    ch = slice(g * P, (g + 1) * P)
                    last = mm(bank[g][:, 0:TOK], up_gate[0:mg, ch], lw[0:mg, 1], start=True, stop=True)
                    if l:
                        last = mm(bank[g][:, TOK:2 * TOK], up_vres[0:mg, ch], lw[0:mg, 1], start=True,
                                  stop=True)
                    last.then_inc(s["upB_mm"], 1)
                pe.wait_ge(s["kksq_done"], l + 1)
                pe.wait_ge(s["sb_copied"], 10 * l + 10)
                for i in range(2):
                    last = mm(bank[4 + i][:], heads1[:], rn[:, 2 * i:2 * i + 2], start=True, stop=True)
                last.then_inc(s["kkn_mm"], 1)
                if l:
                    pe.wait_ge(s["v_ready"], 1)
                for c in range(2):
                    for g in range(G):
                        last = nc.tensor.transpose(bank[6 + c][:, g * P:(g + 1) * P],
                                                   vtile(l, g)[:, c * P:(c + 1) * P], ident[:])
                    last.then_inc(s["tok_mm"], 1)
                pe.wait_ge(s["rr_done"], l + 1)
                pe.wait_ge(s["nn_done"], l + 1)
                for i in range(2):
                    last = mm(bank[4 + i][:], heads1[:], rkv[:, 2 * i:2 * i + 2], start=True, stop=True)
                last.then_inc(s["bonus_mm"], 1)
                pe.wait_ge(s["bkzr_done"], l + 1)
                pe.wait_ge(s["bonus_done"], l + 1)
                for i, src in enumerate((icl, rkv[:, 4:8])):
                    for g in range(G):
                        last = nc.tensor.transpose(bank[4 + i][:, g * P:(g + 1) * P], src[:, g, 0:P],
                                                   ident[:])
                    last.then_inc(s["tok_mm"], 1)
                pe.wait_ge(s["gate_done"], (l + 1) * G)
                pe.wait_ge(s["tok_ready"], 4 * l + 4)

                def scores(g):
                    if g % 2:
                        pe.wait_ge(s["score_ready"], l * G + g)
                    elif g:
                        pe.wait_ge(s["yT_act"], 2 * l + 1)
                        pe.wait_ge(s["yT_dve"], 2 * l + 1)
                    for hh in range(2):
                        ch = slice(hh * HD, (hh + 1) * HD)
                        for c in range(2):
                            tok = slice(c * P, (c + 1) * P)
                            p = 2 * hh + c
                            mm(bank[p][:, 0:2 * P], icl[ch, g, tok], zr[ch, g, c], start=True, stop=True)
                            mm(bank[p][:, 2 * P:4 * P], rkv[ch, 4 + g, tok], zr[ch, g, c], start=True,
                               stop=True)
                            last = mm(bank[4 + hh][:, tok], zr[ch, g, c, 0], icl[ch, g, tok], start=True,
                                      stop=True)
                    last.then_inc(s["score_mm"], 1)

                def sb_scores(hd):
                    ch, g = slice((hd % 2) * HD, (hd % 2 + 1) * HD), hd // 2
                    z, q, k = bank[6 + hd % 2], sbqk[ch, g], sbqk[ch, G + g]
                    return [(z[:, 0:TOK], k[:, 0:P], q), (z[:, TOK:384], k[:, P:TOK], q[:, P:TOK])]

                def sb_z(hd):
                    if hd >= 2:
                        pe.wait_ge(s["o_copied"], l * NSB + hd - 1)
                    for o, kt, q in sb_scores(hd):
                        last = mm(o, kt, q, start=True, stop=True)
                    last.then_inc(s["z_mm"], 1)

                def sb_arg(hd):
                    pe.wait_ge(s["spm_done"], l * NSB + hd + 1)
                    (o0, k0, q0), (o1, k1, q1) = sb_scores(hd)
                    sp_ = sbt[:, hd % 2]
                    mm(o0[:, 0:P], k0, q0[:, 0:P], start=True, stop=False)
                    mm(o0[:, 0:P], neg_low[:], sp_[:, 0:P], start=False, stop=True)
                    mm(o0[:, P:TOK], k0, q0[:, P:TOK], start=True, stop=False)
                    mm(o0[:, P:TOK], neg_low[:], sp_[:, P:TOK], start=False, stop=False)
                    mm(o0[:, P:TOK], neg_ones[:], sp_[:, TOK:384], start=False, stop=True)
                    mm(o1, k1, q1, start=True, stop=False)
                    mm(o1, neg_low[:], sp_[:, TOK:384], start=False, stop=True).then_inc(s["arg_mm"], 1)

                def sb_o(hd):
                    pe.wait_ge(s["att_exp"], l * NSB + hd + 1)
                    ch = slice((hd % 2) * HD, (hd % 2 + 1) * HD)
                    o, att = bank[6 + hd % 2], sbt[:, hd % 2]
                    v0, v1 = (sbv[:, t, hd * HD:(hd + 1) * HD] for t in range(TT))
                    mm(o[ch, 0:P], v0, att[:, 0:P], start=True, stop=True)
                    mm(o[ch, P:TOK], v0, att[:, P:TOK], start=True, stop=False)
                    mm(o[ch, P:TOK], v1, att[:, TOK:384], start=False, stop=True).then_inc(s["o_mm"], 1)

                for pair in range(2):
                    for r in range(2):
                        scores(2 * pair + r)
                    for level in range(1, LEVELS):
                        slot = pair * (LEVELS - 1) + level - 1
                        for r in range(2):
                            n = merge_no(l, pair, level, r)
                            if level == 1:
                                pe.wait_ge(s["score_ready"], l * G + 2 * pair + 2)
                            else:
                                pe.wait_ge(s["d_ready"], n - 1)
                            pe.wait_ge(s["asT_done"], n + 1)
                            for p in range(4):
                                last = mm(bank[3 * r][:, p * P:(p + 1) * P], asT[:, r, p], dd[:, r, p],
                                          start=True, stop=True)
                            last.then_inc(s["y_mm"], 1)
                        if 0 <= slot - 2 < NSB:
                            sb_o(slot - 2)
                        for r in range(2):
                            n = merge_no(l, pair, level, r)
                            pe.wait_ge(s["y_copied"], n + 1)
                            for p in range(4):
                                cl = slice(p * P, (p + 1) * P)
                                if level < LEVELS - 1:
                                    mm(bank[3 * r + 1][:, cl], dT[:, r, p], ysb[:, r, p], start=True,
                                       stop=True)
                                last = mm(bank[3 * r + 2][:, cl], ysb[:, r, p], dT[:, r, p], start=True,
                                          stop=True)
                            last.then_inc(s["g_mm"], 1)
                        if slot < NSB:
                            sb_z(slot)
                        if 0 <= slot - 1 < NSB:
                            sb_arg(slot - 1)
                    base = pair_no(l, pair)
                    heads = [(r, hh) for r in range(2) for hh in range(2)]
                    vcol = lambda r, hh: slice(((2 * pair + r) * 2 + hh) * HD, ((2 * pair + r) * 2 + hh + 1) * HD)
                    q4 = lambda r, hh: slice((2 * r + hh) * HD, (2 * r + hh + 1) * HD)
                    pe.wait_ge(s["d_ready"], merge_no(l, pair, LEVELS - 1, 1) + 1)
                    for r, hh in heads:
                        last = mm(bank[0][:, q4(r, hh)], sc[:, r, 2 * hh, 2 * P:3 * P],
                                  vtok[:, 0, vcol(r, hh)], start=True, stop=True)
                    last.then_inc(s["solve_mm"], 1)
                    pe.wait_ge(s["solve_act"], 4 * base + 1)
                    for r, hh in heads:
                        last = mm(bank[1][:, q4(r, hh)], dT[:, r, 2 * hh], wsb[:, 0, 2 * r + hh],
                                  start=True, stop=True)
                    last.then_inc(s["solve_mm"], 1)
                    pe.wait_ge(s["solve_act"], 4 * base + 2)
                    for hh in range(2):
                        ch = slice(hh * HD, (hh + 1) * HD)
                        for r in range(2):
                            o = bank[2 + hh][ch, r * HD:(r + 1) * HD]
                            mm(o, bktok[:, 0, vcol(r, hh)], usb[:, 0, 2 * r + hh], start=True, stop=False)
                            last = mm(o, bktok[:, 1, vcol(r, hh)], vtok[:, 0, vcol(r, hh)], start=False,
                                      stop=True)
                    last.then_inc(s["solve_mm"], 1)
                    pe.wait_ge(s["solve_dve"], base + 1)
                    for hh in range(2):
                        ch = slice(hh * HD, (hh + 1) * HD)
                        for r in range(2):
                            o = bank[4 + hh][:, r * HD:(r + 1) * HD]
                            mm(o, sc[:, r, 2 * hh + 1, 2 * P:3 * P], vtok[:, 1, vcol(r, hh)], start=True,
                               stop=False)
                            last = mm(o, zr[ch, 2 * pair + r, 1, 0], s1[ch, r], start=False, stop=True)
                    last.then_inc(s["solve_mm"], 1)
                    pe.wait_ge(s["solve_act"], 4 * base + 3)
                    for r, hh in heads:
                        last = mm(bank[0][:, q4(r, hh)], dT[:, r, 2 * hh + 1], wsb[:, 1, 2 * r + hh],
                                  start=True, stop=True)
                    last.then_inc(s["solve_mm"], 1)
                    pe.wait_ge(s["solve_act"], 4 * base + 4)
                    for hh in range(2):
                        ch = slice(hh * HD, (hh + 1) * HD)
                        for r in range(2):
                            for c in range(2):
                                o = bank[1 + hh][ch, (2 * r + c) * P:(2 * r + c + 1) * P]
                                p = 2 * hh + c
                                mm(o, usb[:, c, 2 * r + hh], sc[:, r, p, P:2 * P], start=True, stop=False)
                                last = mm(o, vtok[:, c, vcol(r, hh)], sc[:, r, p, 3 * P:4 * P],
                                          start=False, stop=c == 0)
                                if c:
                                    last = mm(o, s1[ch, r], zr[ch, 2 * pair + r, 1, 1], start=False,
                                              stop=True)
                    last.then_inc(s["solve_mm"], 1)

                pe.wait_ge(s["yT_act"], 2 * (l + 1))
                pe.wait_ge(s["yT_dve"], 2 * (l + 1))
                for i in range(2):
                    mm(bank[i][:], heads64[:], yo[:, 2 * i:2 * i + 2], start=True, stop=True
                       ).then_inc(s["mean_mm"], 1)
                pe.wait_ge(s["sq2_done"], l + 1)
                for i in range(4):
                    mm(bank[2 + i][:], heads64[:], sq2[:, i * 512:(i + 1) * 512], start=True, stop=True
                       ).then_inc(s["var_mm"], 1)
                for half in range(2):
                    loaded(7 + half)
                    for t in range(TT):
                        for n, k in enumerate(list(range(G, KD)) + list(range(G))):
                            pe.wait_ge(s["mixed"], l * KD + n + 1)
                            last = mm(bank[half * 2 + t][:], yo[:, k, t * P:(t + 1) * P], W(7 + half)[:, k],
                                      start=n == 0, stop=n == KD - 1)
                        last.then_inc(s["wo_mm"], 1)

            def gu_products(q, u, v, slot, wait_split, tile, wait_bank):
                if wait_split:
                    pe.wait_ge(q.gu_lo, 2 * tile + 1)
                if wait_bank:
                    pe.wait_ge(q.h_done, u - 1)
                t = v if q.T == 2 else 0
                for k in range(KD):
                    if wait_split and k == KD // 2:
                        pe.wait_ge(q.gu_lo, 2 * tile + 2)
                    hi = xT_hi[:, k, t * P:(t + 1) * P]
                    lo = xT_lo[:, k, t * P:(t + 1) * P] if q.T == 2 else xg_lo[:, k]
                    mm(bank[v][:], hi, gu_hi[:, slot, k], start=k == 0, stop=False)
                    mm(bank[v][:], hi, gu_lo[:, slot, k], start=False, stop=False)
                    last = mm(bank[v][:], lo, gu_hi[:, slot, k], start=False, stop=k == KD - 1)
                last.then_inc(q.gu_mm, 1)

            def transposes(q, u, v):
                pe.wait_ge(q.h_done, u + 1)
                for c in range(2):
                    last = nc.tensor.transpose(bank[2 + v][:, c * P:(c + 1) * P], h[:, v, c * P:(c + 1) * P],
                                               ident[:])
                last.then_inc(q.tr_mm, 1)

            def down_products(q, u, v, slot, tile, wait_split, first, final):
                pe.wait_ge(q.hT_lo, u + 1)
                if wait_split:
                    pe.wait_ge(q.d_lo, tile + 1 + q.credit)
                y0 = 4 + 2 * (v if q.T == 2 else 0)
                for half in range(2):
                    cl = slice(half * 512, (half + 1) * 512)
                    for c in range(2):
                        o = bank[y0 + half][:]
                        st, fi = first and c == 0, final and c == 1
                        mm(o, hT_hi[:, v, c], d_hi[:, slot, c, cl], start=st, stop=False)
                        mm(o, hT_hi[:, v, c], d_lo[:, slot, c, cl], start=False, stop=False)
                        last = mm(o, hT_lo[:, v, c], d_hi[:, slot, c, cl], start=False, stop=fi)
                last.then_inc(q.dn_mm, 1)

            def tiles(q, f0, load0, u0, local, next_split=True):
                for w in range(2):
                    slot = (w + q.slot0) % 2
                    for t in range(q.T):
                        i = w * q.T + t
                        v, u, ul = i % 2, u0 + i, local * q.T + i
                        gu_products(q, u, v, slot, t == 0, f0 + w, ul >= 2)
                        if ul >= 1:
                            if ul >= 3:
                                pe.wait_ge(q.hT_lo, u - 1)
                            transposes(q, u - 1, 1 - v)
                        if ul >= 2:
                            back = 2 // q.T
                            down_products(q, u - 2, v, (w - back + q.slot0) % 2, f0 + w - back, t == 0,
                                          ul - 2 < q.T, False)

            def tiles_end(q, u_end, f_end):
                pe.wait_ge(q.hT_lo, u_end - 1)
                transposes(q, u_end - 1, 1)
                slot_last = (NF - 1 + q.slot0) % 2
                slot_prev = slot_last if q.T == 2 else 1 - slot_last
                down_products(q, u_end - 2, 0, slot_prev, f_end - 2 // q.T, True, False, True if q.T == 2
                              else False)
                down_products(q, u_end - 1, 1, slot_last, f_end - 1, q.T == 1, False, True)

            norm(0)
            mixer(0)
            norm(1)
            pe.wait_ge(s["xT_dve"], 12)
            tiles(ff, 0, 0, 0, 0)
            with pe.Fori(1, NF // 2 - 1) as j:
                tiles(ff, 2 * j, j, 4 * j, 2)
            tiles(ff, NF - 2, None, 2 * NF - 4, 2)
            tiles_end(ff, 2 * NF, NF)
            norm(2)
            mixer(1)
            norm(3)
            pe.wait_ge(s["xT_act"], 20)
            pe.wait_ge(s["xT_dve"], 20)
            pe.wait_ge(s["router_loaded"], 16)
            for t in range(TT):
                for k in range(KD):
                    last = mm(bank[6][:, t * NE:(t + 1) * NE], xnT[:, k, t * P:(t + 1) * P], router[:, k],
                              start=k == 0, stop=k == KD - 1)
            last.then_inc(s["router_mm"], 1)
            pe.wait_ge(s["picks_done"], 1)
            picked = route[:, 6].rearrange("p (t e) -> p t e", t=TT)
            mm(bank[7][:, 0:NE], up_mask[:, 1], picked[:, 0], start=True, stop=True)
            mm(bank[7][:, NE:2 * NE], ones[:], picked[:, 0], start=True, stop=False)
            mm(bank[7][:, NE:2 * NE], up_mask[:, 1], picked[:, 1], start=False, stop=True)
            mm(bank[7][:, 32:32 + NE], ones[:], picked[:, 0], start=True, stop=False)
            mm(bank[7][:, 32:32 + NE], ones[:], picked[:, 1], start=False, stop=True
               ).then_inc(s["counts_mm"], 1)
            pe.wait_ge(s["hn_ready"], 1)
            pe.wait_ge(s["table_ready"], 1)
            n_items = pe.value_load(table[0:1, 12:13], min_val=NE, max_val=MAX_ITEMS)
            with pe.Fori(0, n_items) as i:
                pe.wait_ge(s["sel_done"], i + 1)
                for b in range(2):
                    for kk_ in range(4):
                        k = 4 * b + kk_
                        for t in range(TT):
                            last = mm(bank[6 + b][:, kk_ * P:(kk_ + 1) * P], xn[:, t, k * P:(k + 1) * P],
                                      sel[:, t], start=t == 0, stop=t == TT - 1)
                    last.then_inc(s["gather_mm"], 1)
                for t in range(TT):
                    last = nc.tensor.transpose(bank[2][:, t * P:(t + 1) * P], selg[:, t], ident[:])
                last.then_inc(s["sel_t_mm"], 1)
                pe.wait_ge(s["xg_lo"], i * 2 + 2)
                pe.wait_ge(s["sel_t_done"], i + 1)
                moe_tiles(pe, tiles, i)
                tiles_end(moe, i * NF + NF, i * NF + NF)
                pe.wait_ge(s["y_evicted"], i * 2 + 2)
                for t in range(TT):
                    for half in range(2):
                        k = 2 * t + half
                        mm(bank[(6, 7, 2, 3)[k]][:], selT[:, t], y_sb[:, half * 512:(half + 1) * 512],
                           start=True, stop=True).then_inc(s["scatter_mm"], 1)


def kernel(**inputs):
    import concourse.bacc as bacc
    from concourse.bass_utils import run_bass_kernel_spmd

    nc = bacc.Bacc("TRN2", target_bir_lowering=False, num_devices=1)
    arrays, aps = {}, {}
    for name in INPUTS:
        array = np.ascontiguousarray(inputs[name])
        arrays["in_" + name] = array
        aps[name] = nc.dram_tensor("in_" + name, array.shape, mybir.dt.from_np(array.dtype),
                                   kind="ExternalInput").ap()
    out = nc.dram_tensor("out_0", (1, TOK, D), F32, kind="ExternalOutput").ap()
    build(nc, aps, out)
    result = run_bass_kernel_spmd(nc, [arrays], core_ids=[0])
    return result.results[0]["out_0"]
```
